# Optimizing a Trainium2 kernel written in Bass

```python
import math
import jax
import jax.numpy as jnp
from jax import lax
import numpy as np

D_MODEL = 1024
BATCH = 1
SEQ = 512
DEPTH = 1

MEM_LEN = 256
EPS = 1e-6
DA_HEADS = 4
DA_DIM = 64
DA_VDIM = 2 * DA_DIM
GLA_HEADS = 4
GLA_DK = 64
GLA_DV = 128
GLA_RANK = 16
GLA_TAU = 16.0
GLA_CHUNK = 64
MIX_WIDTH = DA_HEADS * DA_VDIM + GLA_HEADS * GLA_DV
ROPE_THETA = 500000.0
ROPE_DIM = DA_DIM // 4
Q_BLOCK = 128
X_HEADS = 4
X_DIM = D_MODEL // X_HEADS
N_EXPERTS = 32
TOP_K = 4
D_FF = D_MODEL
SWIGLU_LIMIT = 7.0
SWIGLU_ALPHA = 1.702
MOE_BLOCK = 128
DA_QK = DA_HEADS * 2 * DA_DIM
DA_V = DA_HEADS * DA_VDIM
G_QK = GLA_HEADS * GLA_DK
G_V = GLA_HEADS * GLA_DV
SPLITS = (DA_QK, DA_QK, DA_V, G_QK, G_QK, G_V, G_V, GLA_RANK)
IN_WIDTH = 2 * DA_QK + DA_V + 2 * G_QK + 2 * G_V + GLA_RANK

kernel_name = 'hymba_style_diffattn_gla_moe_block'

def rms_norm(x, g):
    xf = x.astype(jnp.float32)
    y = xf * lax.rsqrt(jnp.mean(xf * xf, axis=-1, keepdims=True) + EPS)
    return (y * g.astype(jnp.float32)).astype(x.dtype)

def partial_rope(t, positions):
    half = ROPE_DIM // 2
    inv_freq = ROPE_THETA ** (-jnp.arange(0, ROPE_DIM, 2, dtype=jnp.float32) / ROPE_DIM)
    ang = positions.astype(jnp.float32)[..., None] * inv_freq
    cos = jnp.cos(ang)[:, :, None, None, :]
    sin = jnp.sin(ang)[:, :, None, None, :]
    tf = t.astype(jnp.float32)
    x1, x2 = tf[..., :half], tf[..., half:ROPE_DIM]
    rot = jnp.concatenate([x1 * cos - x2 * sin, x2 * cos + x1 * sin, tf[..., ROPE_DIM:]], axis=-1)
    return rot.astype(t.dtype)

def diff_attention(q, k, v, lam, positions):
    S = q.shape[1]
    q = partial_rope(q, positions) * (DA_DIM ** -0.5)
    k = partial_rope(k, positions)
    outs = []
    for i in range(S // Q_BLOCK):
        q0 = i * Q_BLOCK
        kend = q0 + Q_BLOCK
        s = jnp.einsum('bqhcd,bkhcd->bhcqk', q[:, q0:kend], k[:, :kend]).astype(jnp.float32)
        mask = (q0 + jnp.arange(Q_BLOCK))[:, None] >= jnp.arange(kend)[None, :]
        p = jax.nn.softmax(jnp.where(mask, s, -jnp.inf), axis=-1)
        a = p[:, :, 0] - lam * p[:, :, 1]
        outs.append(jnp.einsum('bhqk,bkhe->bqhe', a.astype(v.dtype), v[:, :kend]))
    return jnp.concatenate(outs, axis=1)

def gla_chunked(q, k, v, log_a):
    B, S, H, dk = q.shape
    dv = v.shape[-1]
    C = GLA_CHUNK
    n = S // C

    def to_chunks(t):
        return t.reshape(B, n, C, H, t.shape[-1]).transpose(1, 0, 3, 2, 4)

    qc, kc, vc, gc = (to_chunks(t) for t in (q * (dk ** -0.5), k, v, log_a))
    causal = jnp.tril(jnp.ones((C, C), dtype=bool))[:, :, None]

    def step(state, inp):
        qi, ki, vi, gi = inp
        b = jnp.cumsum(gi, axis=2)
        inter = jnp.einsum('bhtd,bhde->bhte', qi * jnp.exp(b), state)
        diff = b[:, :, :, None, :] - b[:, :, None, :, :]
        decay = jnp.exp(jnp.where(causal, diff, -jnp.inf))
        attn = jnp.einsum('bhtd,bhsd,bhtsd->bhts', qi, ki, decay)
        intra = jnp.einsum('bhts,bhse->bhte', attn, vi)
        b_last = b[:, :, -1:, :]
        new_state = state * jnp.exp(b_last[:, :, 0, :, None]) + jnp.einsum(
            'bhsd,bhse->bhde', ki * jnp.exp(b_last - b), vi)
        return new_state, inter + intra

    state0 = jnp.zeros((B, H, dk, dv), jnp.float32)
    _, out = lax.scan(step, state0, (qc, kc, vc, gc))
    return out.transpose(1, 0, 3, 2, 4).reshape(B, S, H, dv)

def hybrid_mixer(h, positions, w_in, lambda_q1, lambda_k1, lambda_q2, lambda_k2,
                 diff_norm_g, w_alpha2, b_alpha, gla_norm_g, w_out, lambda_init):
    B, S, _ = h.shape
    proj = h @ w_in
    idx = [int(c) for c in np.cumsum(SPLITS)[:-1]]
    dq, dk_, dv_, gq, gk, gv, gr, ga = jnp.split(proj, idx, axis=-1)
    lam = (jnp.exp(jnp.sum(lambda_q1.astype(jnp.float32) * lambda_k1.astype(jnp.float32)))
           - jnp.exp(jnp.sum(lambda_q2.astype(jnp.float32) * lambda_k2.astype(jnp.float32)))
           + lambda_init)
    o_da = diff_attention(dq.reshape(B, S, DA_HEADS, 2, DA_DIM),
                          dk_.reshape(B, S, DA_HEADS, 2, DA_DIM),
                          dv_.reshape(B, S, DA_HEADS, DA_VDIM), lam, positions)
    o_da = (rms_norm(o_da, diff_norm_g) * (1.0 - lambda_init)).reshape(B, S, DA_V)
    log_a = jax.nn.log_sigmoid((ga @ w_alpha2 + b_alpha).astype(jnp.float32)) / GLA_TAU
    o_gla = gla_chunked(gq.reshape(B, S, GLA_HEADS, GLA_DK).astype(jnp.float32),
                        gk.reshape(B, S, GLA_HEADS, GLA_DK).astype(jnp.float32),
                        gv.reshape(B, S, GLA_HEADS, GLA_DV).astype(jnp.float32),
                        log_a.reshape(B, S, GLA_HEADS, GLA_DK))
    o_gla = rms_norm(o_gla, gla_norm_g) * jax.nn.silu(gr.reshape(B, S, GLA_HEADS, GLA_DV).astype(jnp.float32))
    o_gla = o_gla.reshape(B, S, G_V).astype(h.dtype)
    return jnp.concatenate([o_da, o_gla], axis=-1) @ w_out

def memory_cross_attention(h, m, w_cq, w_ck, w_cv, w_co):
    B, S, D = h.shape
    M = m.shape[1]
    q = (h @ w_cq).reshape(B, S, X_HEADS, X_DIM)
    k = (m @ w_ck).reshape(B, M, X_HEADS, X_DIM)
    v = (m @ w_cv).reshape(B, M, X_HEADS, X_DIM)
    s = jnp.einsum('bqhd,bkhd->bhqk', q, k).astype(jnp.float32) * (X_DIM ** -0.5)
    p = jax.nn.softmax(s, axis=-1)
    o = jnp.einsum('bhqk,bkhd->bqhd', p.astype(v.dtype), v).reshape(B, S, D)
    return o @ w_co

def moe_ffn(h, w_router, b_router, w_up, b_up, w_down, b_down):
    B, S, D = h.shape
    N = B * S
    A = N * TOP_K
    t = h.reshape(N, D)
    logits = (t @ w_router + b_router).astype(jnp.float32)
    top_logit, top_e = lax.top_k(logits, TOP_K)
    gate = jax.nn.softmax(top_logit, axis=-1).reshape(A)
    flat_e = top_e.reshape(A)
    order = jnp.argsort(flat_e)
    sorted_e = flat_e[order]
    tok = order // TOP_K
    counts = jnp.bincount(flat_e, length=N_EXPERTS)
    padded = (counts + MOE_BLOCK - 1) // MOE_BLOCK * MOE_BLOCK
    start = jnp.cumsum(counts) - counts
    pad_end = jnp.cumsum(padded)
    pad_start = pad_end - padded
    dest = pad_start[sorted_e] + jnp.arange(A) - start[sorted_e]
    cap = A + N_EXPERTS * MOE_BLOCK
    n_blk = cap // MOE_BLOCK
    x_pad = jnp.zeros((cap, D), t.dtype).at[dest].set(t[tok])
    blk_e = jnp.minimum(jnp.searchsorted(pad_end, jnp.arange(n_blk) * MOE_BLOCK, side='right'),
                        N_EXPERTS - 1)

    def expert_block(args):
        xb, e = args
        u = xb @ w_up[e] + b_up[e]
        glu = jnp.minimum(u[:, :D_FF], SWIGLU_LIMIT)
        lin = jnp.clip(u[:, D_FF:], -SWIGLU_LIMIT, SWIGLU_LIMIT)
        act = glu * jax.nn.sigmoid(SWIGLU_ALPHA * glu) * (lin + 1.0)
        return act @ w_down[e] + b_down[e]

    y_pad = lax.map(expert_block, (x_pad.reshape(n_blk, MOE_BLOCK, D), blk_e))
    y = y_pad.reshape(cap, D)[dest] * gate[order][:, None].astype(t.dtype)
    return jax.ops.segment_sum(y, tok, num_segments=N).reshape(B, S, D)

def setup_inputs(seed: int = 0) -> dict:
    key = jax.random.key(seed)
    ks = jax.random.split(key, 32)
    L = DEPTH
    f32 = jnp.float32

    def nrm(k, shape, scale):
        return jax.random.normal(k, shape, f32) * scale

    def gain(k, shape):
        return 1.0 + 0.02 * jax.random.normal(k, shape, f32)

    return {
        'x': nrm(ks[0], (BATCH, SEQ, D_MODEL), 1.0),
        'mem': nrm(ks[1], (BATCH, MEM_LEN, D_MODEL), 1.0),
        'positions': (jnp.arange(SEQ, dtype=jnp.int32)[None, :]
                      + jax.random.randint(ks[2], (BATCH, 1), 0, 4096, dtype=jnp.int32)),
        'norm_mix_g': gain(ks[3], (L, D_MODEL)),
        'w_in': nrm(ks[4], (L, D_MODEL, IN_WIDTH), D_MODEL ** -0.5),
        'lambda_q1': nrm(ks[5], (L, DA_DIM), 0.1),
        'lambda_k1': nrm(ks[6], (L, DA_DIM), 0.1),
        'lambda_q2': nrm(ks[7], (L, DA_DIM), 0.1),
        'lambda_k2': nrm(ks[8], (L, DA_DIM), 0.1),
        'diff_norm_g': gain(ks[9], (L, DA_VDIM)),
        'w_alpha2': nrm(ks[10], (L, GLA_RANK, G_QK), GLA_RANK ** -0.5),
        'b_alpha': nrm(ks[11], (L, G_QK), 0.1),
        'gla_norm_g': gain(ks[12], (L, GLA_DV)),
        'w_out': nrm(ks[13], (L, MIX_WIDTH, D_MODEL), MIX_WIDTH ** -0.5),
        'norm_cross_g': gain(ks[14], (L, D_MODEL)),
        'norm_mem_g': gain(ks[15], (L, D_MODEL)),
        'w_cq': nrm(ks[16], (L, D_MODEL, D_MODEL), D_MODEL ** -0.5),
        'w_ck': nrm(ks[17], (L, D_MODEL, D_MODEL), D_MODEL ** -0.5),
        'w_cv': nrm(ks[18], (L, D_MODEL, D_MODEL), D_MODEL ** -0.5),
        'w_co': nrm(ks[19], (L, D_MODEL, D_MODEL), D_MODEL ** -0.5),
        'norm_ffn_g': gain(ks[20], (L, D_MODEL)),
        'w_router': nrm(ks[21], (L, D_MODEL, N_EXPERTS), D_MODEL ** -0.5),
        'b_router': nrm(ks[22], (L, N_EXPERTS), 0.01),
        'w_up': nrm(ks[23], (L, N_EXPERTS, D_MODEL, 2 * D_FF), D_MODEL ** -0.5),
        'b_up': nrm(ks[24], (L, N_EXPERTS, 2 * D_FF), 0.01),
        'w_down': nrm(ks[25], (L, N_EXPERTS, D_FF, D_MODEL), D_FF ** -0.5),
        'b_down': nrm(ks[26], (L, N_EXPERTS, D_MODEL), 0.01),
        'norm_final_g': gain(ks[27], (D_MODEL,)),
    }

def reference(x, mem, positions, norm_mix_g, w_in, lambda_q1, lambda_k1, lambda_q2, lambda_k2,
              diff_norm_g, w_alpha2, b_alpha, gla_norm_g, w_out, norm_cross_g, norm_mem_g,
              w_cq, w_ck, w_cv, w_co, norm_ffn_g, w_router, b_router, w_up, b_up, w_down, b_down,
              norm_final_g):
    for l in range(DEPTH):
        lambda_init = 0.8 - 0.6 * math.exp(-0.3 * l)
        x = x + hybrid_mixer(rms_norm(x, norm_mix_g[l]), positions, w_in[l],
                             lambda_q1[l], lambda_k1[l], lambda_q2[l], lambda_k2[l],
                             diff_norm_g[l], w_alpha2[l], b_alpha[l], gla_norm_g[l], w_out[l],
                             lambda_init)
        x = x + memory_cross_attention(rms_norm(x, norm_cross_g[l]), rms_norm(mem, norm_mem_g[l]),
                                       w_cq[l], w_ck[l], w_cv[l], w_co[l])
        x = x + moe_ffn(rms_norm(x, norm_ffn_g[l]), w_router[l], b_router[l],
                        w_up[l], b_up[l], w_down[l], b_down[l])
    return rms_norm(x, norm_final_g)


_drawn_inputs = setup_inputs


def setup_inputs(seed=0):
    import zlib

    import numpy as np

    out = dict(_drawn_inputs(seed))
    spreads = {}
    factors = {'lambda_q1': 46.641,
     'gla_norm_g': 2.883,
     'norm_cross_g': 4.335,
     'norm_mem_g': 4.145,
     'b_up': 37.494,
     'b_down': 43.303,
     'norm_final_g': 9.683,
     'norm_ffn_g': 5.272,
     'b_router': 7.898}
    for name, (base, spread) in spreads.items():
        noise = np.random.default_rng([zlib.crc32(name.encode()), seed]).standard_normal(out[name].shape)
        drawn = base * np.exp(spread * noise) if base else spread * noise
        out[name] = jnp.asarray(drawn.astype(out[name].dtype))
    for name, factor in factors.items():
        out[name] = (out[name] * factor).astype(out[name].dtype)
    return out
```

```python
import math
from contextlib import ExitStack

import concourse.bass as bass
from concourse import mybir
from concourse.alu_op_type import AluOpType as ALU

F32 = mybir.dt.float32
BF16 = mybir.dt.bfloat16
I32 = mybir.dt.int32
U32 = mybir.dt.uint32
ACT = mybir.ActivationFunctionType
AX = mybir.AxisListType

P = 128
SLOTS = 128
EPS = 1e-6
LAMBDA_INIT = 0.8 - 0.6 * math.exp(-0.3 * 0)
ROPE_THETA, ROPE_DIM = 500000.0, 16
RH = ROPE_DIM // 2
GLA_TAU = 16.0
LIMIT, ALPHA = 7.0, 1.702
GUARD = 85.0
NEG = -1e30
RING = 6
OOB = 4096.0
TWO_PI = 2 * math.pi
PI_A = 6.28125
PI_B = 0.0019350051879882812
PI_C = TWO_PI - PI_A - PI_B
ROUND = 12582912.0
G_MIX, G_CROSS, G_MEM, G_FFN, G_DA, G_GLA, G_BA = 0, 8, 16, 24, 32, 33, 34


class Steps:

    def __init__(self, sem):
        self.sem, self.n, self.base = sem, 0, 0

    def mark(self, ins):
        ins.then_inc(self.sem, 1)
        self.n += 1

    def wait(self, eng):
        eng.wait_ge(self.sem, self.base + self.n)


def plan_steps():
    steps = [("gains",), ("norm", "mix"), ("lam",), ("angles",)]
    steps += [("proj", "q", b) for b in range(4)]
    steps += [("proj", "k", b) for b in range(4)]
    steps += [("rope", 0), ("rope", 1)]
    steps += [("proj", "g", m) for m in range(4)]
    steps += [("qkT", s, h) for h in range(4) for s in range(2)]
    steps += [("ga",), ("gate_z", 0), ("gate_z", 1)]
    steps += [("proj", "v", b) for b in range(4)]
    steps += [("gla_decay", 0), ("norm_mem",), ("gla_decay", 1)]
    filler = [("proj", "gv", b) for b in range(4)] + [("proj", "gr", b) for b in range(4)]
    filler += [("proj", "kx", m) for m in range(8)]
    filler += [("proj", "vx", m) for m in range(4)]
    gla = []
    for c in range(4):
        gla += [[("gla_scores", c, t), ("gla_kd", c, t)][:2 if c < 3 else 1] for t in range(2)]
        gla += [[("gla_out", c, t), ("gla_state", c, t)][:2 if c < 3 else 1] for t in range(2)]
    for n in range(16 + 4):
        if n < 16:
            steps.append(("scores", n))
        if 0 <= n - 1 < 16:
            steps.append(("combine", n - 1))
        if 0 <= n - 2 < 16:
            steps.append(("attnT", n - 2))
        if 0 <= n - 3 < 16:
            steps.append(("attnV", n - 3))
        if filler:
            steps.append(filler.pop(0))
        if n >= 6 and gla:
            steps += gla.pop(0)
    while gla or filler:
        if filler:
            steps.append(filler.pop(0))
        if gla:
            steps += gla.pop(0)
    steps += [("mix_norm",), ("oT",)]
    steps += [("proj", "wo", n) for n in range(8)]
    steps += [("norm", "cross")]
    steps += [("proj", "qx", m) for m in range(8)]
    for h in range(5):
        if h < 4:
            steps += [("xscores", h, i) for i in range(4)]
        if h >= 1:
            steps += [("xT", h - 1, mb) for mb in range(2)]
            steps += [("xout", h - 1, ec) for ec in range(2)]
    steps += [("proj", "co", n) for n in range(8)]
    steps += [("norm", "ffn"), ("router",), ("route",)]
    return steps


def decoder_block(nc, A, slots=SLOTS):
    T, D = A["x"].shape[1], A["x"].shape[2]
    NB, KT = T // P, D // P
    M = A["mem"].shape[1]
    MB = M // P
    NE = A["w_router"].shape[2]
    FF = A["w_down"].shape[2]
    TOP = 4
    W = slots
    MO = NE * (T // W - 1) if W > P else (T * TOP // (W + 1) + 1)
    PANELS = FF // 256
    h_rows = nc.dram_tensor("h_rows", [T, D], F32, kind="Internal").ap()
    acc_rows = nc.dram_tensor("acc_rows", [T, D], F32, kind="Internal").ap()
    steps = plan_steps()

    first_col = {"q": 0, "k": 512, "v": 1024, "g": 1536, "gv": 2048, "gr": 2560}
    square = {"kx": "w_ck", "vx": "w_cv", "wo": "w_out", "qx": "w_cq", "co": "w_co"}
    per_group = {"vx": 2}
    groups = []
    for s in steps:
        if s[0] == "proj":
            g = (s[1], 0 if s[1] in first_col else s[2] // per_group.get(s[1], 4))
            if g not in groups:
                groups.append(g)
    DENSE = 2 * len(groups)
    PER_EXPERT = 2 * PANELS + 4
    assert PER_EXPERT % RING == 0

    with ExitStack() as ctx:
        def sb(name, shape, dt=F32):
            return ctx.enter_context(nc.sbuf_tensor(name, shape, dt))

        def sem(name):
            return ctx.enter_context(nc.semaphore(name))

        bank = [ctx.enter_context(nc.psum_tensor(f"bank{b}", [P, 512], F32)) for b in range(8)]

        ring = sb("ring", [P, RING, 4, 512])
        x_res = sb("x_res", [P, NB, D])
        actT = sb("actT", [P, KT, T])
        tokA = sb("tokA", [P, NB, D])
        arena = sb("arena", [P, 21 * 1024 + 512])
        pbuf = sb("pbuf", [P, 2, 512])
        abuf = sb("abuf", [P, 2, 512])
        aT = sb("aT", [P, 2, 512])
        gsc = sb("gsc", [P, 2, 256])
        junk = gsc.rearrange("p t n -> p (t n)").bitcast(BF16)
        junk_o = sb("junk_o", [P, P], BF16)
        small = sb("small", [P, 480])
        gcol = sb("gcol", [P, 40])
        ident = sb("ident", [P, P])
        negmask = sb("negmask", [P, P])
        keepT = sb("keepT", [P, P])
        ones = sb("ones", [P, P])
        ones_bf = sb("ones_bf", [P, P], BF16)
        before = sb("before", [P, P], BF16)
        part_of = sb("part_of", [P, NE])
        iota_e = sb("iota_e", [P, NE])
        slot_rank = sb("slot_rank", [P, NB, NE + 1])
        slot_src = sb("slot_src", [P, NB, NE + 1, 5], BF16)
        pos_i = sb("pos_i", [P, NB], I32)
        idx8 = sb("idx8", [P, NB, 8], U32)
        lamrow = abuf[0:1, 0, 0:5 * 64]
        grow = abuf[0:36, 1, 0:P]
        w_ga = aT[:, 0, 0:16 * KT].rearrange("p (k n) -> p k n", k=KT)
        w_al = sb("w_al", [16, 256])
        w_rt = abuf[:, 1, 0:KT * NE].rearrange("p (k n) -> p k n", k=KT)
        state = sb("state", [P, 2, P])
        kd_tok = sb("kd_tok", [P, 2, P])
        count_f = sb("count_f", [1, NE])
        count_i = sb("count_i", [1, 1], I32)
        ovf_tmp = sb("ovf_tmp", [1, 2 * NE + 2 * MO])
        ovf_n, ovf_upto = ovf_tmp[:, 0:NE], ovf_tmp[:, NE:2 * NE]
        ovf_e, ovf_j = ovf_tmp[:, 2 * NE:2 * NE + MO], ovf_tmp[:, 2 * NE + MO:]
        pbuf_row = pbuf[0:1, :, :].rearrange("p u n -> p (u n)")[:, 0:MO * NE]
        abuf_row = abuf[0:1, :, :].rearrange("p u n -> p (u n)")[:, 0:MO * NE]
        ovf = sb("ovf", [1, 2 * MO + 1], I32)

        at = [0]

        def carve(words, pattern=None, **kw):
            a = arena[:, at[0]:at[0] + words]
            at[0] += words
            return a.rearrange(pattern, **kw) if pattern else a

        v_tok = carve(NB * 512, "p (b n) -> p b n", b=NB)
        gv_tok = carve(NB * 512, "p (b n) -> p b n", b=NB)
        gr_tok = carve(NB * 512, "p (b n) -> p b n", b=NB)
        at_qk = at[0]
        qT = carve(4 * T, "p (h n) -> p h n", h=4)
        kT = carve(4 * T, "p (h n) -> p h n", h=4)
        at_gla = at[0]
        gqkT = carve(4 * T, "p (m n) -> p m n", m=4)
        decay = carve(2 * T, "p (m n) -> p m n", m=2)
        qE = carve(2 * T, "p (m n) -> p m n", m=2)
        kE = carve(2 * T, "p (m n) -> p m n", m=2)
        memT = carve(KT * M, "p (k n) -> p k n", k=KT)
        at_kx = at[0]
        kxT = carve(KT * M, "p (k n) -> p k n", k=KT)
        vx = carve(MB * D, "p (b n) -> p b n", b=MB)
        assert at[0] <= 21 * 1024 + 512
        mem_x = arena[:, at_kx:at_kx + MB * D].rearrange("p (b n) -> p b n", b=MB)
        qxT = arena[:, at_qk:at_qk + KT * T].rearrange("p (k n) -> p k n", k=KT)
        xp = v_tok.rearrange("p b n -> p (b n)").rearrange("p (u i n) -> p u i n", u=2, i=4)
        xpT = gv_tok.rearrange("p b n -> p (b n)").rearrange("p (u m n) -> p u m n", u=2, m=2)
        gffn = gr_tok.rearrange("p b n -> p (b n)")[:, 0:D]
        ebuf = aT
        gaT = pbuf[0:16, 0, :]
        lgT = pbuf[0:NE, 0, :]
        bias_src = arena[:, at_gla:at_gla + 3 * FF]
        bias_bf = arena[:, at_gla + 3 * FF:at_gla + 3 * FF + 3 * FF // 2].bitcast(BF16)

        at[0] = 0
        xg = carve(D)
        xT = carve(KT * W, "p (k n) -> p k n", k=KT)
        glu = carve(512, "p (u n) -> p u n", u=2)
        lin = carve(512, "p (u n) -> p u n", u=2)
        sig = carve(512, "p (u n) -> p u n", u=2)
        act_tok = carve(512, "p (u n) -> p u n", u=2)
        hT = carve(KT * W, "p (k n) -> p k n", k=KT)
        y_tok = carve(D)
        onehot = carve(NB * W // 2).bitcast(BF16).rearrange("p (b n) -> p b n", b=NB)
        sel = carve(W // 2).bitcast(BF16)
        idx_next, idx_cur = carve(1).bitcast(U32), carve(1).bitcast(U32)
        gate_next, gate_cur, idx_f = carve(1), carve(1), carve(1)
        gfin = carve(D)
        iota_s = carve(512)
        assert at[0] <= at_gla

        sp = [0]

        def cols(n):
            a = small[:, sp[0]:sp[0] + n]
            sp[0] += n
            return a

        eps_c, ss, rstd, mss, mrstd = cols(1), cols(4), cols(4), cols(2), cols(2)
        nmax, psum_, rec = cols(32), cols(32), cols(32)
        nlam, lam2, lam1 = cols(1), cols(2), cols(1)
        oss, orstd = cols(32), cols(32)
        pos_f, br_c, part_f = cols(NB), cols(1), cols(1)
        lg, m_f, g_f = [aT[:, 0, P * q:P * q + P].rearrange("p (b e) -> p b e", b=NB) for q in range(3)]
        slot_m = aT[:, 1, 0:P // 2].bitcast(BF16).rearrange("p (b e) -> p b e", b=NB)
        mx8, idxf, gate4 = cols(NB * 8), cols(NB * TOP), cols(NB * TOP)
        gsum, dstate, ifreq = cols(NB), cols(8), cols(RH)
        scratch = cols(160)
        ang = scratch[:, 0:32]
        turns = scratch[:, 32:64]
        red = scratch[:, 64:96]
        sin_t, cos_t = scratch[:, 96:128], scratch[:, 128:160]

        bank_full = [sem(f"bank_full{b}") for b in range(8)]
        bank_free = [sem(f"bank_free{b}") for b in range(8)]
        chunk_in = [sem(f"chunk_in{s}") for s in range(RING)]
        chunk_used = sem("chunk_used")
        mem_in, gains_in, small_in, bias_in, gfin_in = [sem(n) for n in (
            "mem_in", "gains_in", "small_in", "bias_in", "gfin_in")]
        gathers, scatters = sem("gathers"), sem("scatters")
        pe_step = sem("pe_step")
        pool_step, dve_step, act_step = sem("pool_step"), sem("dve_step"), sem("act_step")
        consts_ready = sem("consts_ready")
        gcol_ready = sem("gcol_ready")
        rstd_ready, xn_ready, actT_ready = sem("rstd_ready"), sem("xn_ready"), sem("actT_ready")
        mrstd_ready, memn_ready, memT_ready = sem("mrstd_ready"), sem("memn_ready"), sem("memT_ready")
        lam_sums, lam_exps, lam_ready = sem("lam_sums"), sem("lam_exps"), sem("lam_ready")
        angles_ready, trig_ready = sem("angles_ready"), sem("trig_ready")
        qk_raw, roped, qT_ready, kT_ready = sem("qk_raw"), sem("roped"), sem("qT_ready"), sem("kT_ready")
        gqk_ready, ga_ready, z_ready = sem("gqk_ready"), sem("ga_ready"), sem("z_ready")
        abs_ready, softplus_ready, expo_ready, decays_ready, gla_ready = [sem(n) for n in (
            "abs_ready", "softplus_ready", "expo_ready", "decays_ready", "gla_ready")]
        v_ready, gv_ready, gr_exp, gr_ready = sem("v_ready"), sem("gv_ready"), sem("gr_exp"), sem("gr_ready")
        kx_ready, vx_ready, qx_ready = sem("kx_ready"), sem("vx_ready"), sem("qx_ready")
        max_ready, p_ready, a_ready, aT_ready = sem("max_ready"), sem("p_ready"), sem("a_ready"), sem("aT_ready")
        gsc_ready, kd_ready, state_ready = sem("gsc_ready"), sem("kd_ready"), sem("state_ready")
        o_ready, orstd_ready, mixed_ready = sem("o_ready"), sem("orstd_ready"), sem("mixed_ready")
        res_ready = sem("res_ready")
        xmax_ready, xp_raw, xp_ready, xpT_ready = sem("xmax_ready"), sem("xp_raw"), sem("xp_ready"), sem("xpT_ready")
        lgT_ready, gexp_in, gexp_ready, m_ready, slots_ready = [sem(n) for n in (
            "lgT_ready", "gexp_in", "gexp_ready", "m_ready", "slots_ready")]
        rows_out, bias_ready = sem("rows_out"), sem("bias_ready")
        onehot_ready, sel_ready, idx_done, idx_ready = [sem(n) for n in (
            "onehot_ready", "sel_ready", "idx_done", "idx_ready")]
        xg_zero, xg_in, xgT_done, xgT_free, xT_ready = [sem(n) for n in (
            "xg_zero", "xg_in", "xgT_done", "xgT_free", "xT_ready")]
        up_full, up_free, glu_ready, sig_ready, act_ready = [sem(n) for n in (
            "up_full", "up_free", "glu_ready", "sig_ready", "act_ready")]
        hT_done, hT_ready, down_full, y_ready, added = [sem(n) for n in (
            "hT_done", "hT_ready", "down_full", "y_ready", "added")]
        cur_ready, table_ready = sem("cur_ready"), sem("table_ready")
        router_in, iota_ready = sem("router_in"), sem("iota_ready")
        gffn_in, cur_free = sem("gffn_in"), sem("cur_free")
        fin_in = [sem(f"fin_in{b}") for b in range(NB)]
        x_in = [sem(f"x_in{b}") for b in range(NB)]
        fin_rstd, fin_ready, out_done = sem("fin_rstd"), sem("fin_ready"), sem("out_done")
        ovf_step, dve_prep, dve_main = sem("ovf_step"), sem("dve_prep"), sem("dve_main")

        dve, act, pool, tensor = Steps(dve_step), Steps(act_step), Steps(pool_step), Steps(pe_step)

        job_at, jobs_on, turn = {}, [0] * 8, {"proj": 0, "work": 0}
        several = {"norm": range(KT), "norm_mem": range(0, KT, 2), "oT": range(KT), "scores": range(2),
                   "router": ("logitsT", "logits"), "route": ("rank", "count")}
        for s in steps:
            if s[0] in ("rope", "gla_decay", "mix_norm", "combine", "angles"):
                continue
            for name in ([s + (k,) for k in several[s[0]]] if s[0] in several else [s]):
                kind = "proj" if s[0] == "proj" else "work"
                b = turn[kind] % 4 + (0 if kind == "proj" else 4)
                turn[kind] += 1
                job_at[name] = (b, jobs_on[b])
                jobs_on[b] += 1

        def ps(job):
            return bank[job_at[job][0]]

        def begin(eng, job):
            b, k = job_at[job]
            if k:
                eng.wait_ge(bank_free[b], k)

        def finish(ins, job):
            ins.then_inc(bank_full[job_at[job][0]], 1)

        def ready(eng, job):
            b, k = job_at[job]
            eng.wait_ge(bank_full[b], k + 1)

        def release(ins, job):
            ins.then_inc(bank_free[job_at[job][0]], 1)

        def evac(eng, own_steps, ins, job, done):
            own_steps.mark(ins)
            own_steps.wait(eng)
            eng.sem_inc(bank_free[job_at[job][0]], 1)
            eng.sem_inc(done, 1)

        def act_evac(eng, ins, job, done):
            evac(eng, act, ins, job, done)

        def dve_evac(eng, ins, job, done):
            evac(eng, dve, ins, job, done)

        def xnormal(v, s, n):
            h, i = n // 4, n % 4
            v.wait_ge(xp_raw, n + 1)
            dve.mark(v.reciprocal(rec[:, n:n + 1], psum_[:, n:n + 1]))
            dve.wait(v)
            v.tensor_scalar(xp[:, h % 2, i, :], xp[:, h % 2, i, :], rec[:, n:n + 1], None, ALU.mult).then_inc(xp_ready, 1)

        N_CONST = 12 + RH
        NORMS = {"mix": (0, G_MIX, 0), "cross": (1, G_CROSS, 2), "ffn": (2, G_FFN, 4)}

        block = ctx.enter_context(nc.Block())

        def expert_chunk(c, e):
            if c < 2 * PANELS:
                w = A["w_up"][0].rearrange("e (k p) (g f) -> e p k g f", p=P, g=2)
                return [(g, w[e, :, 4 * (c % 2):4 * (c % 2) + 4, g, 256 * (c // 2):256 * (c // 2) + 256]) for g in range(2)]
            c -= 2 * PANELS
            w = A["w_down"][0].rearrange("e (k p) n -> e p k n", p=P)
            return [(None, w[e, :, 4 * (c // 2):4 * (c // 2) + 4, 512 * (c % 2):512 * (c % 2) + 512])]

        UP_DMAS = 2
        def slot_incs(c):
            return 16 * UP_DMAS if c < 2 * PANELS else 16

        slot_total = [sum(slot_incs(c) for c in range(s, PER_EXPERT, RING)) for s in range(RING)]
        slot_upto = [sum(slot_incs(c2) for c2 in range(c % RING, c + 1, RING)) for c in range(PER_EXPERT)]
        slot_dense = [16 * len(range(s, DENSE, RING)) for s in range(RING)]

        def expert_chunk_in(eng, n, c):
            eng.wait_ge(chunk_in[c % RING], slot_dense[c % RING] + slot_total[c % RING] * n + slot_upto[c])

        group_jobs = {}
        for st in steps:
            if st[0] == "proj":
                group_jobs[(st[1], 0 if st[1] in first_col else st[2] // per_group.get(st[1], 4))] = st

        @block.sync
        def _(sp_):
            chunk = 0
            for name, g in groups:
                for half in range(2):
                    src = A["w_in"] if name in first_col else A[square[name]]
                    c0 = first_col[name] if name in first_col else 512 * g
                    if chunk >= RING:
                        ready(sp_, group_jobs[groups[(chunk - RING) // 2]])
                    w = src[0].rearrange("(k p) n -> p k n", p=P)[:, 4 * half:4 * half + 4, c0:c0 + 512]
                    sp_.dma_start(ring[:, chunk % RING, :, :], w).then_inc(chunk_in[chunk % RING], 16)
                    chunk += 1
            ready(sp_, group_jobs[groups[-1]])
            sp_.sem_inc(chunk_used, RING)

            def load_expert(n, e):
                for c in range(PER_EXPERT):
                    sp_.wait_ge(chunk_used, n * PER_EXPERT + (c + 1))
                    for g, w in expert_chunk(c, e):
                        dst = ring[:, c % RING, :, :]
                        if g is not None:
                            dst = dst[:, :, 256 * g:256 * g + 256]
                        sp_.dma_start(dst, w).then_inc(chunk_in[c % RING], 16)

            with sp_.Fori(0, NE) as e:
                load_expert(e, e)
            sp_.wait_ge(table_ready, 1)
            extra = sp_.value_load(ovf[0:1, 2 * MO:2 * MO + 1], min_val=0, max_val=MO)
            with sp_.If(extra > 0):
                with sp_.Fori(0, extra) as m:
                    e = sp_.value_load(ovf[0:1, bass.ds(m, 1)], min_val=0, max_val=NE - 1)
                    load_expert(m + NE, e)
            for b in range(NB):
                sp_.wait_ge(fin_ready, b + 1)
                sp_.dma_start(A["out"][0, P * b:P * b + P, :], x_res[:, b, :]).then_inc(out_done, 16)
            sp_.wait_ge(out_done, 16 * NB)

        @block.gpsimd
        def _(g):
            def made(ins):
                pool.mark(ins)
                pool.wait(g)

            def const(ins):
                ins.then_inc(consts_ready, 1)
            made(g.memset(ident[:, :], 0.0))
            const(g.affine_select(out=ident[:, :], in_=ident[:, :], compare_op=ALU.not_equal, fill=1.0,
                                  base=0, pattern=[[-1, P]], channel_multiplier=1))
            const(g.memset(eps_c, EPS))
            const(g.memset(ones[:, :], 1.0))
            const(g.memset(ones_bf[:, :], 1.0))
            for j in range(RH):
                const(g.memset(ifreq[:, j:j + 1], ROPE_THETA ** (-2.0 * j / ROPE_DIM)))
            made(g.memset(negmask[:, :], 0.0))
            const(g.affine_select(out=negmask[:, :], in_=negmask[:, :], compare_op=ALU.is_ge, fill=NEG,
                                  base=0, pattern=[[-1, P]], channel_multiplier=1))
            made(g.memset(keepT[:, :], 1.0))
            const(g.affine_select(out=keepT[:, :], in_=keepT[:, :], compare_op=ALU.is_ge, fill=0.0,
                                  base=0, pattern=[[1, P]], channel_multiplier=-1))
            made(g.memset(before[:, :], 1.0))
            const(g.affine_select(out=before[:, :], in_=before[:, :], compare_op=ALU.is_gt, fill=0.0,
                                  base=0, pattern=[[1, P]], channel_multiplier=-1))
            made(g.memset(part_of[:, :], 0.0))
            for q in range(3):
                ins = g.affine_select(out=part_of[:, :], in_=part_of[:, :], compare_op=ALU.not_equal, fill=1.0,
                                      base=-32 * q, pattern=[[-1, NE]], channel_multiplier=1)
                const(ins) if q == 2 else made(ins)
            const(g.iota(iota_e[:, :], pattern=[[1, NE]], base=0, channel_multiplier=0,
                         allow_small_or_imprecise_dtypes=True))
            const(g.iota(part_f, pattern=[[0, 1]], base=0, channel_multiplier=1,
                         allow_small_or_imprecise_dtypes=True))
            const(g.memset(slot_rank[:, :, :], -1.0))
            const(g.memset(slot_src[:, :, :, :], 0.0))
            g.wait_ge(mixed_ready, NB)
            g.dma_start(w_rt[:, :, :], A["w_router"][0].rearrange("(k p) n -> p k n", p=P)).then_inc(router_in, 16)
            for q in range(3):
                g.dma_start(bias_src[32 * q:32 * q + 32, 0:2 * FF], A["b_up"][0]).then_inc(bias_in, 16)
                g.dma_start(bias_src[32 * q:32 * q + 32, 2 * FF:3 * FF], A["b_down"][0]).then_inc(bias_in, 16)
            made(g.memset(bias_bf[96:128, :], 0.0))
            g.wait_ge(bias_in, 16 * 6)
            made(g.tensor_copy(bias_bf[0:96, :], bias_src[0:96, :]))
            made(g.tensor_tensor(bias_src[0:96, :], bias_src[0:96, :], bias_bf[0:96, :], ALU.subtract))
            made(g.tensor_copy(bias_bf[32:64, :], bias_src[32:64, :]))
            made(g.tensor_copy(bias_bf[64:96, :], bias_src[64:96, :]))
            made(g.tensor_tensor(bias_src[64:96, :], bias_src[64:96, :], bias_bf[64:96, :], ALU.subtract))
            g.tensor_copy(bias_bf[64:96, :], bias_src[64:96, :]).then_inc(bias_ready, 1)
            g.dma_start(gffn, A["norm_ffn_g"].partition_broadcast(P)).then_inc(gffn_in, 16)
            g.wait_ge(bias_ready, 1)
            g.wait_ge(xn_ready, 2 * NB + 1)
            g.iota(iota_s, pattern=[[1, 512]], base=0, channel_multiplier=0,
                   allow_small_or_imprecise_dtypes=True).then_inc(iota_ready, 1)
            for b in range(NB):
                g.wait_ge(xn_ready, 2 * NB + b + 1)
                g.dma_start(h_rows[P * b:P * b + P, :], tokA[:, b, :]).then_inc(rows_out, 16)
                g.dma_start(acc_rows[P * b:P * b + P, :], x_res[:, b, :]).then_inc(rows_out, 16)
            g.wait_ge(slots_ready, 1)
            g.wait_ge(iota_ready, 1)
            g.memset(xg, 0.0).then_inc(xg_zero, 1)
            g.wait_ge(xg_zero, 1)
            g.wait_ge(rows_out, 16 * 2 * NB)
            g.dma_start(gfin, A["norm_final_g"].rearrange("(o n) -> o n", o=1).partition_broadcast(P)).then_inc(gfin_in, 16)
            g.sem_inc(cur_free, 1)

            def gather(n):
                g.wait_ge(idx_ready, n + 1)
                g.sem_inc(gathers, 1)
                g.indirect_dma_start(out=xg[0:W, :], out_offset=None, in_=h_rows,
                                     in_offset=bass.IndirectOffsetOnAxis(ap=idx_next[0:W, :], axis=0),
                                     bounds_check=T - 1, oob_is_err=False).then_inc(xg_in, 16)

            def scatter(n):
                g.wait_ge(y_ready, 2 * n + 4)
                g.sem_inc(scatters, 1)
                g.indirect_dma_start(out=acc_rows, in_=y_tok[0:W, :],
                                     out_offset=bass.IndirectOffsetOnAxis(ap=idx_cur[0:W, :], axis=0), in_offset=None,
                                     bounds_check=T - 1, oob_is_err=False,
                                     compute_op=ALU.add).then_inc(added, 16)
                g.wait_ge(added, 16 * n + 16)
                g.sem_inc(cur_free, 1)

            gather(0)
            with g.Fori(0, NE) as e:
                g.wait_ge(xgT_done, e + 1)
                gather(e + 1)
                scatter(e)
            g.wait_ge(xgT_done, NE + 1)
            g.wait_ge(table_ready, 1)
            extra = g.value_load(ovf[0:1, 2 * MO:2 * MO + 1], min_val=0, max_val=MO)
            with g.If(extra > 0):
                with g.Fori(0, extra) as m:
                    gather(m + NE + 1)
                    scatter(m + NE)
            for b in range(NB):
                g.dma_start(x_res[:, b, :], acc_rows[P * b:P * b + P, :]).then_inc(fin_in[b], 16)

        @block.tensor
        def _(pe):
            pe.wait_ge(consts_ready, 1)
            chunk = [0]
            group_of = {}

            def own(ins):
                tensor.mark(ins)
                tensor.wait(pe)

            def proj(s):
                name, m = s[1], s[2]
                g = (name, 0 if name in first_col else m // per_group.get(name, 4))
                if g not in group_of:
                    group_of[g] = chunk[0]
                    chunk[0] += 2
                c0 = group_of[g]
                stage = {"wo": 2, "qx": 3, "co": 4}.get(name, 1)
                if name in ("kx", "vx"):
                    pe.wait_ge(memT_ready, KT // 2)
                else:
                    pe.wait_ge(actT_ready, 8 * stage)
                begin(pe, s)
                for half in range(2):
                    c = c0 + half
                    pe.wait_ge(chunk_in[c % RING], 16 * (c // RING + 1))
                    for kk in range(4):
                        k = 4 * half + kk
                        w = ring[:, c % RING, kk, :]
                        if name in ("g", "qx"):
                            lhsT, rhs, o = w[:, P * (m % 4):P * (m % 4) + P], actT[:, k, :], ps(s)[:, :]
                        elif name == "kx":
                            lhsT, rhs, o = w[:, P * (m % 4):P * (m % 4) + P], memT[:, k, :], ps(s)[:, 0:M]
                        elif name == "vx":
                            lhsT, rhs, o = memT[:, k, P * (m % 2):P * (m % 2) + P], w, ps(s)[:, :]
                        else:
                            lhsT, rhs, o = actT[:, k, P * (m % 4):P * (m % 4) + P], w, ps(s)[:, :]
                        mm = pe.matmul(o, lhsT, rhs, start=(k == 0), stop=(k == KT - 1))
                finish(mm, s)

            for s in steps:
                kind = s[0]
                if kind == "proj":
                    proj(s)
                elif kind == "gains":
                    pe.wait_ge(gains_in, 16 * 7)
                    begin(pe, s)
                    finish(pe.transpose(ps(s)[:, 0:36], grow[:, :], ident[0:36, 0:36]), s)
                elif kind == "norm":
                    n = NORMS[s[1]][0]
                    pe.wait_ge(xn_ready, NB * (n + 1))
                    for k in range(KT):
                        begin(pe, s + (k,))
                        for b in range(NB):
                            t = pe.transpose(ps(s + (k,))[:, P * b:P * b + P], tokA[:, b, P * k:P * k + P], ident[:, :])
                        finish(t, s + (k,))
                elif kind == "norm_mem":
                    pe.wait_ge(memn_ready, MB)
                    for k in range(0, KT, 2):
                        begin(pe, s + (k,))
                        for k2 in range(2):
                            for b in range(MB):
                                t = pe.transpose(ps(s + (k,))[:, M * k2 + P * b:M * k2 + P * b + P],
                                                 mem_x[:, b, P * (k + k2):P * (k + k2) + P], ident[:, :])
                        finish(t, s + (k,))
                elif kind == "lam":
                    pe.wait_ge(lam_ready, 1)
                    begin(pe, s)
                    finish(pe.matmul(ps(s)[:, 0:1], ones[0:1, :], lam1[0:1, :], start=True, stop=True), s)
                elif kind == "qkT":
                    pe.wait_ge(roped, s[1] + 1)
                    begin(pe, s)
                    for b in range(NB):
                        c0 = 512 * s[1] + P * s[2]
                        t = pe.transpose(ps(s)[:, P * b:P * b + P], tokA[:, b, c0:c0 + P], ident[:, :])
                    finish(t, s)
                elif kind == "ga":
                    pe.wait_ge(small_in, 16 * 8)
                    begin(pe, s)
                    for k in range(KT):
                        mm = pe.matmul(ps(s)[0:16, :], w_ga[:, k, :], actT[:, k, :], start=(k == 0), stop=(k == KT - 1))
                    finish(mm, s)
                elif kind == "gate_z":
                    pe.wait_ge(ga_ready, 1)
                    begin(pe, s)
                    finish(pe.matmul(ps(s)[:, :], w_al[:, P * s[1]:P * s[1] + P], gaT, start=True, stop=True), s)
                elif kind == "scores":
                    h, i = s[1] // 4, s[1] % 4
                    pe.wait_ge(qT_ready, h + 1)
                    pe.wait_ge(kT_ready, h + 1)
                    for c in range(2):
                        j = s + (c,)
                        begin(pe, j)
                        finish(pe.matmul(ps(j)[:, 0:P * (i + 1)], qT[64 * c:64 * c + 64, h, P * i:P * i + P],
                                         kT[64 * c:64 * c + 64, h, 0:P * (i + 1)], start=True, stop=True), j)
                elif kind == "attnT":
                    n, i = s[1], s[1] % 4
                    pe.wait_ge(a_ready, n + 1)
                    begin(pe, s)
                    for j in range(i + 1):
                        t = pe.transpose(ps(s)[:, P * j:P * j + P], abuf[:, n % 2, P * j:P * j + P], ident[:, :])
                    finish(t, s)
                elif kind == "attnV":
                    n, h, i = s[1], s[1] // 4, s[1] % 4
                    pe.wait_ge(v_ready, NB)
                    pe.wait_ge(aT_ready, n + 1)
                    begin(pe, s)
                    for j in range(i + 1):
                        mm = pe.matmul(ps(s)[:, 0:P], aT[:, n % 2, P * j:P * j + P], v_tok[:, j, P * h:P * h + P],
                                       start=(j == 0), stop=(j == i))
                    finish(mm, s)
                elif kind == "gla_scores":
                    c, t = s[1], s[2]
                    pe.wait_ge(gla_ready, t + 1)
                    begin(pe, s)
                    for hh in range(2):
                        r = slice(64 * hh, 64 * hh + 64)
                        mm = pe.matmul(ps(s)[:, P * hh:P * hh + P], kE[r, t, P * c:P * c + P], qE[r, t, P * c:P * c + P],
                                       start=True, stop=True)
                        if hh == 0:
                            own(mm)
                    finish(mm, s)
                elif kind == "gla_kd":
                    c, t = s[1], s[2]
                    begin(pe, s)
                    finish(pe.transpose(ps(s)[:, 0:P], gqkT[:, 2 + t, P * c:P * c + P], ident[:, :]), s)
                elif kind == "gla_out":
                    c, t = s[1], s[2]
                    pe.wait_ge(gsc_ready, 2 * c + t + 1)
                    pe.wait_ge(gv_ready, c + 1)
                    if c:
                        pe.wait_ge(state_ready, 2 * (2 * (c - 1) + t + 1))
                    begin(pe, s)
                    for hh in range(2):
                        r, hd = slice(64 * hh, 64 * hh + 64), 2 * t + hh
                        mm = pe.matmul(ps(s)[:, P * hh:P * hh + P], gsc[:, t, P * hh:P * hh + P],
                                       gv_tok[:, c, P * hd:P * hd + P], start=True, stop=(c == 0))
                        if c:
                            mm = pe.matmul(ps(s)[:, P * hh:P * hh + P], gqkT[r, t, P * c:P * c + P], state[r, t, :],
                                           start=False, stop=True)
                            if hh == 0:
                                own(mm)
                    finish(mm, s)
                elif kind == "gla_state":
                    c, t = s[1], s[2]
                    pe.wait_ge(kd_ready, 2 * c + t + 1)
                    begin(pe, s)
                    finish(pe.matmul(ps(s)[:, 0:256], kd_tok[:, t, :], gv_tok[:, c, 256 * t:256 * t + 256],
                                     start=True, stop=True), s)
                elif kind == "oT":
                    pe.wait_ge(mixed_ready, NB)
                    for k in range(KT):
                        begin(pe, s + (k,))
                        for b in range(NB):
                            t = pe.transpose(ps(s + (k,))[:, P * b:P * b + P], tokA[:, b, P * k:P * k + P], ident[:, :])
                        finish(t, s + (k,))
                elif kind == "xscores":
                    h, i = s[1], s[2]
                    pe.wait_ge(qx_ready, 2 * h + 2)
                    pe.wait_ge(kx_ready, KT)
                    begin(pe, s)
                    for kk in range(2):
                        mm = pe.matmul(ps(s)[:, 0:M], qxT[:, 2 * h + kk, P * i:P * i + P], kxT[:, 2 * h + kk, :],
                                       start=(kk == 0), stop=(kk == 1))
                    finish(mm, s)
                elif kind == "xT":
                    h, mb = s[1], s[2]
                    pe.wait_ge(xp_ready, 4 * h + 4)
                    begin(pe, s)
                    for i in range(NB):
                        t = pe.transpose(ps(s)[:, P * i:P * i + P], xp[:, h % 2, i, P * mb:P * mb + P], ident[:, :])
                    finish(t, s)
                elif kind == "xout":
                    h, ec = s[1], s[2]
                    pe.wait_ge(xpT_ready, 2 * h + 2)
                    pe.wait_ge(vx_ready, 4)
                    begin(pe, s)
                    for mb in range(MB):
                        c0 = 256 * h + P * ec
                        mm = pe.matmul(ps(s)[:, :], vx[:, mb, c0:c0 + P], xpT[:, h % 2, mb, :],
                                       start=(mb == 0), stop=(mb == MB - 1))
                    finish(mm, s)
                elif kind == "router":
                    pe.wait_ge(actT_ready, 8 * 5)
                    pe.wait_ge(router_in, 16)
                    j = s + ("logitsT",)
                    begin(pe, j)
                    for k in range(KT):
                        mm = pe.matmul(ps(j)[0:NE, :], w_rt[:, k, :], actT[:, k, :], start=(k == 0), stop=(k == KT - 1))
                    finish(mm, j)
                    pe.wait_ge(lgT_ready, 1)
                    j = s + ("logits",)
                    begin(pe, j)
                    for b in range(NB):
                        t = pe.transpose(ps(j)[:, NE * b:NE * b + NE], lgT[:, P * b:P * b + P], ident[0:NE, 0:NE])
                    finish(t, j)
                elif kind == "route":
                    pe.wait_ge(m_ready, 1)
                    j = s + ("rank",)
                    begin(pe, j)
                    for b in range(NB):
                        for b2 in range(b + 1):
                            mm = pe.matmul(ps(j)[:, NE * b:NE * b + NE], before[:, :] if b2 == b else ones_bf[:, :],
                                           slot_m[:, b2, :], start=(b2 == 0), stop=(b2 == b))
                    finish(mm, j)
                    j = s + ("count",)
                    begin(pe, j)
                    for b in range(NB):
                        mm = pe.matmul(ps(j)[:, 0:NE], ones_bf[:, :], slot_m[:, b, :], start=(b == 0), stop=(b == NB - 1))
                    finish(mm, j)

            for b in range(8):
                pe.wait_ge(bank_free[b], jobs_on[b])
            pe.sem_inc(down_full, 2)

            def index(pn, e):
                pe.wait_ge(onehot_ready, pn + 1)
                for b in range(NB):
                    mm = pe.matmul(bank[7][0:W, 0:5], onehot[:, b, :], slot_src[:, b, e, :],
                                   start=(b == 0), stop=(b == NB - 1))
                mm.then_inc(idx_done, 1)

            def rows_T(pn):
                pe.wait_ge(xg_in, 16 * pn + 16)
                for half in range(2):
                    for kk in range(4):
                        t = pe.transpose(bank[6 + half][:, W * kk:W * kk + W],
                                         xg[0:W, P * (4 * half + kk):P * (4 * half + kk) + P], ident[0:W, 0:W])
                t.then_inc(xgT_done, 1)

            def hidden_T(n, p):
                pe.wait_ge(act_ready, n * PANELS + (p + 1))
                for kk in range(2):
                    t = pe.transpose(bank[6 + p % 2][:, W * kk:W * kk + W], act_tok[0:W, p % 2, P * kk:P * kk + P],
                                     ident[0:W, 0:W])
                t.then_inc(hT_done, 1)

            def up(n, p):
                pe.wait_ge(up_free, n * PANELS + (p + 1))
                if p == 0:
                    pe.wait_ge(xT_ready, 2 * n + 2)
                for half in range(2):
                    c = 2 * p + half
                    expert_chunk_in(pe, n, c)
                    for kk in range(4):
                        mm = pe.matmul(bank[p][0:W, :], xT[:, 4 * half + kk, :], ring[:, c % RING, kk, :],
                                       start=(half == 0 and kk == 0), stop=False)
                    mm.then_inc(chunk_used, 1)
                if p == 0:
                    pe.wait_ge(sel_ready, n + 1)
                pe.matmul(bank[p][0:W, :].rearrange("p (g f) -> p g f", g=2), sel,
                          bias_bf[:, 0:2 * FF].rearrange("p (g f) -> p g f", g=2)[:, :, 256 * p:256 * p + 256],
                          start=False, stop=True).then_inc(up_full, 1)

            def down(n, half):
                if half == 0:
                    pe.wait_ge(y_ready, 2 * n + 2)
                pe.wait_ge(hT_ready, n * PANELS + (2 * half + 2))
                for side in range(2):
                    c = 2 * PANELS + 2 * half + side
                    expert_chunk_in(pe, n, c)
                    for kk in range(4):
                        mm = pe.matmul(bank[4 + side][0:W, :], hT[:, 4 * half + kk, :], ring[:, c % RING, kk, :],
                                       start=(half == 0 and kk == 0), stop=False)
                    mm.then_inc(chunk_used, 1)
                    if half == 1:
                        pe.matmul(bank[4 + side][0:W, :], sel, bias_bf[:, 2 * FF + 512 * side:2 * FF + 512 * side + 512],
                                  start=False, stop=True).then_inc(down_full, 1)

            pe.wait_ge(slots_ready, 1)
            pe.wait_ge(bias_ready, 1)
            index(0, 0)
            rows_T(0)
            with pe.Fori(0, NE) as e:
                up(e, 0)
                up(e, 1)
                hidden_T(e, 0)
                index(e + 1, e + 1)
                up(e, 2)
                pe.wait_ge(idx_ready, e + 2)
                hidden_T(e, 1)
                up(e, 3)
                pe.wait_ge(hT_ready, e * PANELS + 1)
                hidden_T(e, 2)
                pe.wait_ge(hT_ready, e * PANELS + 3)
                rows_T(e + 1)
                down(e, 0)
                pe.wait_ge(xT_ready, 2 * e + 4)
                hidden_T(e, 3)
                down(e, 1)
            pe.wait_ge(table_ready, 1)
            extra = pe.value_load(ovf[0:1, 2 * MO:2 * MO + 1], min_val=0, max_val=MO)
            with pe.If(extra > 0):
                with pe.Fori(0, extra) as m:
                    e = pe.value_load(ovf[0:1, bass.ds(m, 1)], min_val=0, max_val=NE - 1)
                    index(m + (NE + 1), e)
                    rows_T(m + (NE + 1))
                    pe.wait_ge(xT_ready, 2 * m + (2 * NE + 4))
                    for p in range(PANELS):
                        up(m + NE, p)
                        if p >= 1:
                            if p == 3:
                                pe.wait_ge(hT_ready, m * PANELS + (NE * PANELS + 1))
                            hidden_T(m + NE, p - 1)
                    down(m + NE, 0)
                    hidden_T(m + NE, 3)
                    down(m + NE, 1)

        @block.scalar
        def _(a):
            for b in range(NB):
                a.dma_start(x_res[:, b, :], A["x"][0, P * b:P * b + P, :]).then_inc(x_in[b], 16)
            for r, name, n in ((G_MIX, "norm_mix_g", 8), (G_CROSS, "norm_cross_g", 8), (G_MEM, "norm_mem_g", 8),
                               (G_FFN, "norm_ffn_g", 8), (G_DA, "diff_norm_g", 1), (G_GLA, "gla_norm_g", 1),
                               (G_BA, "b_alpha", 2)):
                a.dma_start(grow[r:r + n, :], A[name].rearrange("o (k p) -> (o k) p", p=P)).then_inc(gains_in, 16)
            for j, name in enumerate(("lambda_q1", "lambda_k1", "lambda_q2", "lambda_k2")):
                a.dma_start(lamrow[:, 64 * j:64 * j + 64], A[name]).then_inc(small_in, 16)
            a.dma_start(pos_i[:, :], A["positions"].rearrange("o (b p) -> p (o b)", p=P), allow_slow_non_contiguous=True).then_inc(small_in, 16)
            a.dma_start(w_ga[:, :, :], A["w_in"][0].rearrange("(k p) n -> p k n", p=P)[:, :, 3072:3088]).then_inc(small_in, 16)
            a.dma_start(w_al[:, :], A["w_alpha2"][0]).then_inc(small_in, 16)
            a.dma_start(br_c[0:NE, :], A["b_router"].rearrange("o n -> n o"), allow_slow_non_contiguous=True).then_inc(small_in, 16)
            for b in range(MB):
                a.dma_start(mem_x[:, b, :], A["mem"][0, P * b:P * b + P, :]).then_inc(mem_in, 16)

            def own(ins):
                act.mark(ins)
                act.wait(a)

            def rsqrt_mean(dst, src, n, done=None):
                own(a.activation(dst, src, ACT.Ln, scale=1.0 / n, bias=eps_c[0:dst.shape[0], :]))
                ins = a.activation(dst, dst, ACT.Exp, scale=-0.5)
                if done is None:
                    own(ins)
                else:
                    ins.then_inc(done, 1)

            def squares(src, dst):
                own(a.activation(junk[:, 0:src.shape[1]], src, ACT.Square, accum_out=dst))

            a.wait_ge(consts_ready, N_CONST)
            for s in steps:
                kind = s[0]
                if kind == "norm":
                    n = NORMS[s[1]][0]
                    for b in range(NB):
                        if n == 0:
                            a.wait_ge(x_in[b], 16)
                        else:
                            a.wait_ge(res_ready, 8 * n - 8 + 4 + b + 1)
                        squares(x_res[:, b, :], ss[:, b:b + 1])
                    if n:
                        a.wait_ge(xn_ready, NB * n)
                    rsqrt_mean(rstd, ss, D, rstd_ready)
                    for k in range(0, KT, 2):
                        j = s + (k,)
                        ready(a, j)
                        if n == 0:
                            a.wait_ge(gcol_ready, 3)
                        if s[1] == "ffn":
                            ins = a.activation(actT[:, k, :], ps(j)[:, :], ACT.Copy)
                        else:
                            ins = a.activation(actT[:, k, :], ps(j)[:, :], ACT.Copy,
                                               scale=gcol[:, NORMS[s[1]][1] + k:NORMS[s[1]][1] + k + 1])
                        act_evac(a, ins, j, actT_ready)
                elif kind == "norm_mem":
                    a.wait_ge(mem_in, 16 * MB)
                    for b in range(MB):
                        squares(mem_x[:, b, :], mss[:, b:b + 1])
                    rsqrt_mean(mrstd, mss, D, mrstd_ready)
                elif kind == "lam":
                    a.wait_ge(lam_sums, 2)
                    a.activation(lam2[0:1, :], lam2[0:1, :], ACT.Exp).then_inc(lam_exps, 1)
                elif kind == "angles":
                    a.wait_ge(angles_ready, 2)
                    a.activation(sin_t, sin_t, ACT.Sin).then_inc(trig_ready, 1)
                    a.activation(cos_t, cos_t, ACT.Sin).then_inc(trig_ready, 1)
                elif kind == "proj" and s[1] in ("q", "k"):
                    ready(a, s)
                    c0 = 0 if s[1] == "q" else 512
                    act_evac(a, a.activation(tokA[:, s[2], c0:c0 + 512], ps(s)[:, :], ACT.Copy), s, qk_raw)
                elif kind == "proj" and s[1] == "g":
                    ready(a, s)
                    act_evac(a, a.activation(gqkT[:, s[2], :], ps(s)[:, :], ACT.Copy, scale=0.125 if s[2] < 2 else 1.0), s, gqk_ready)
                elif kind == "proj" and s[1] in ("v", "gv"):
                    ready(a, s)
                    dst, done = (v_tok, v_ready) if s[1] == "v" else (gv_tok, gv_ready)
                    act_evac(a, a.activation(dst[:, s[2], :], ps(s)[:, :], ACT.Copy), s, done)
                elif kind == "proj" and s[1] == "gr":
                    ready(a, s)
                    a.activation(gr_tok[:, s[2], :], ps(s)[:, :], ACT.Exp, scale=-1.0).then_inc(gr_exp, 1)
                elif kind == "proj" and s[1] == "vx":
                    ready(a, s)
                    act_evac(a, a.activation(vx[:, s[2] % 2, 512 * (s[2] // 2):512 * (s[2] // 2) + 512], ps(s)[:, :], ACT.Copy), s, vx_ready)
                elif kind == "proj" and s[1] == "qx":
                    ready(a, s)
                    act_evac(a, a.activation(qxT[:, s[2], :], ps(s)[:, :], ACT.Copy, scale=0.0625), s, qx_ready)
                elif kind == "qkT" and s[1] == 0:
                    ready(a, s)
                    act_evac(a, a.activation(qT[:, s[2], :], ps(s)[:, :], ACT.Copy, scale=0.125), s, qT_ready)
                elif kind == "ga":
                    ready(a, s)
                    act_evac(a, a.activation(gaT, ps(s)[0:16, :], ACT.Copy), s, ga_ready)
                elif kind == "gla_decay":
                    t = s[1]
                    a.wait_ge(abs_ready, t + 1)
                    own(a.activation(kE[:, t, :], qE[:, t, :], ACT.Exp, scale=-1.0))
                    a.activation(kE[:, t, :], kE[:, t, :], ACT.Ln, bias=ones[:, 0:1]).then_inc(softplus_ready, 1)
                    a.wait_ge(expo_ready, 2 * t + 1)
                    own(a.activation(qE[:, t, :], kE[:, t, :], ACT.Exp))
                    own(a.activation(kE[:, t, :], kE[:, t, :], ACT.Exp, scale=-1.0))
                    a.wait_ge(expo_ready, 2 * t + 2)
                    own(a.activation(ebuf[:, 0, :], ebuf[:, 0, :], ACT.Exp))
                    a.activation(ebuf[:, 1, :], decay[:, t, :], ACT.Exp).then_inc(decays_ready, 1)
                elif kind == "scores":
                    n, i = s[1], s[1] % 4
                    for c in range(2):
                        j = s + (c,)
                        a.wait_ge(max_ready, 2 * n + c + 1)
                        if n:
                            a.wait_ge(a_ready, n)
                        w = P * (i + 1)
                        ins = a.activation(pbuf[:, c, 0:w], ps(j)[:, 0:w], ACT.Exp, bias=nmax[:, 2 * n + c:2 * n + c + 1],
                                           accum_out=psum_[:, 2 * n + c:2 * n + c + 1])
                        act_evac(a, ins, j, p_ready)
                elif kind == "attnT":
                    n, i = s[1], s[1] % 4
                    ready(a, s)
                    act_evac(a, a.activation(aT[:, n % 2, 0:P * (i + 1)], ps(s)[:, 0:P * (i + 1)], ACT.Copy), s, aT_ready)
                elif kind == "attnV":
                    h, i = s[1] // 4, s[1] % 4
                    ready(a, s)
                    own(a.activation(tokA[:, i, P * h:P * h + P], ps(s)[:, 0:P], ACT.Copy))
                    own(a.activation(junk_o[:, 0:P], ps(s)[:, 0:P], ACT.Square, accum_out=oss[:, 4 * h + i:4 * h + i + 1]))
                    a.sem_inc(bank_free[job_at[s][0]], 1)
                elif kind == "gla_kd":
                    ready(a, s)
                    act_evac(a, a.activation(kd_tok[:, s[2], :], ps(s)[:, 0:P], ACT.Copy), s, kd_ready)
                elif kind == "gla_out":
                    c, t = s[1], s[2]
                    ready(a, s)
                    own(a.activation(tokA[:, c, 512 + 256 * t:768 + 256 * t], ps(s)[:, 0:256], ACT.Copy))
                    for hh in range(2):
                        col_ = 16 + 4 * (2 * t + hh) + c
                        own(a.activation(junk_o[:, 0:P], ps(s)[:, P * hh:P * hh + P], ACT.Square, accum_out=oss[:, col_:col_ + 1]))
                    a.sem_inc(bank_free[job_at[s][0]], 1)
                elif kind == "mix_norm":
                    rsqrt_mean(orstd, oss, P, orstd_ready)
                elif kind == "oT":
                    for k in range(0, KT, 2):
                        j = s + (k,)
                        ready(a, j)
                        gc = G_DA if k < 4 else G_GLA
                        act_evac(a, a.activation(actT[:, k, :], ps(j)[:, :], ACT.Copy, scale=gcol[:, gc:gc + 1]), j, actT_ready)
                elif kind == "xscores":
                    h, i = s[1], s[2]
                    n = 4 * h + i
                    a.wait_ge(xmax_ready, n + 1)
                    act_evac(a, a.activation(xp[:, h % 2, i, :], ps(s)[:, 0:M], ACT.Exp, bias=nmax[:, n:n + 1],
                                             accum_out=psum_[:, n:n + 1]), s, xp_raw)
                elif kind == "xT" and s[2] == 0:
                    ready(a, s)
                    act_evac(a, a.activation(xpT[:, s[1] % 2, 0, :], ps(s)[:, :], ACT.Copy), s, xpT_ready)
                elif kind == "xout" and s[2] == 0:
                    ready(a, s)
                    act_evac(a, a.activation(actT[:, 2 * s[1], :], ps(s)[:, :], ACT.Copy), s, actT_ready)
                elif kind == "router":
                    j = s + ("logitsT",)
                    ready(a, j)
                    act_evac(a, a.activation(lgT, ps(j)[0:NE, :], ACT.Identity, bias=br_c[0:NE, :]), j, lgT_ready)
                elif kind == "route":
                    a.wait_ge(gexp_in, 1)
                    a.activation(gate4, gate4, ACT.Exp).then_inc(gexp_ready, 1)

            def rows_T_out(pn):
                a.wait_ge(xgT_done, pn + 1)
                a.activation(xT[:, 0:4, :], bank[6][:, 0:4 * W].rearrange("p (k n) -> p k n", k=4), ACT.Copy).then_inc(xT_ready, 1)

            def gate(n, p):
                a.wait_ge(glu_ready, n * PANELS + (p + 1))
                a.activation(sig[0:W, p % 2, :], glu[0:W, p % 2, :], ACT.Sigmoid, scale=ALPHA).then_inc(sig_ready, 1)

            def hidden_out(n, p):
                a.wait_ge(hT_done, n * PANELS + (p + 1))
                a.activation(hT[:, 2 * p:2 * p + 2, :], bank[6 + p % 2][:, 0:2 * W].rearrange("p (k n) -> p k n", k=2),
                             ACT.Copy).then_inc(hT_ready, 1)

            def results(n):
                a.wait_ge(cur_ready, n + 1)
                for side in range(2):
                    a.wait_ge(down_full, 2 * n + (side + 3))
                    a.activation(y_tok[0:W, 512 * side:512 * side + 512], bank[4 + side][0:W, :], ACT.Copy,
                                 scale=gate_cur[0:W, :]).then_inc(y_ready, 1)

            a.sem_inc(y_ready, 2)
            rows_T_out(0)
            with a.Fori(0, NE) as e:
                gate(e, 0)
                gate(e, 1)
                hidden_out(e, 0)
                gate(e, 2)
                hidden_out(e, 1)
                gate(e, 3)
                hidden_out(e, 2)
                rows_T_out(e + 1)
                hidden_out(e, 3)
                results(e)
            a.wait_ge(table_ready, 1)
            extra = a.value_load(ovf[0:1, 2 * MO:2 * MO + 1], min_val=0, max_val=MO)
            with a.If(extra > 0):
                with a.Fori(0, extra) as m:
                    rows_T_out(m + (NE + 1))
                    for p in range(PANELS):
                        gate(m + NE, p)
                        if p >= 1:
                            hidden_out(m + NE, p - 1)
                    hidden_out(m + NE, 3)
                    results(m + NE)
            for b in range(NB):
                a.wait_ge(fin_in[b], 16)
                squares(x_res[:, b, :], ss[:, b:b + 1])
                rsqrt_mean(rstd[:, b:b + 1], ss[:, b:b + 1], D, fin_rstd)

        @block.vector
        def _(v):
            def own(ins):
                dve.mark(ins)
                dve.wait(v)

            v.wait_ge(consts_ready, N_CONST)
            for s in steps:
                kind = s[0]
                if kind == "gains":
                    ready(v, s)
                    v.tensor_copy(gcol[:, 0:G_DA], ps(s)[:, 0:G_DA]).then_inc(gcol_ready, 1)
                    v.tensor_scalar(gcol[:, G_DA:G_DA + 1], ps(s)[:, G_DA:G_DA + 1], 1.0 - LAMBDA_INIT, None, ALU.mult).then_inc(gcol_ready, 1)
                    own(v.tensor_copy(gcol[:, G_DA + 1:36], ps(s)[:, G_DA + 1:36]))
                    v.sem_inc(gcol_ready, 1)
                    v.wait_ge(gcol_ready, 3)
                    v.sem_inc(bank_free[job_at[s][0]], 1)
                elif kind == "norm":
                    n = NORMS[s[1]][0]
                    if n == 2:
                        v.wait_ge(gffn_in, 16)
                    v.wait_ge(rstd_ready, n + 1)
                    for b in range(NB):
                        if n == 2:
                            ins = v.scalar_tensor_tensor(out=tokA[:, b, :], in0=x_res[:, b, :], scalar=rstd[:, b:b + 1],
                                                         in1=gffn, op0=ALU.mult, op1=ALU.mult)
                        else:
                            ins = v.tensor_scalar(tokA[:, b, :], x_res[:, b, :], rstd[:, b:b + 1], None, ALU.mult)
                        ins.then_inc(xn_ready, 1)
                    for k in range(1, KT, 2):
                        j = s + (k,)
                        ready(v, j)
                        if s[1] == "ffn":
                            ins = v.tensor_copy(actT[:, k, :], ps(j)[:, :])
                        else:
                            gc = NORMS[s[1]][1] + k
                            ins = v.tensor_scalar(actT[:, k, :], ps(j)[:, :], gcol[:, gc:gc + 1], None, ALU.mult)
                        dve_evac(v, ins, j, actT_ready)
                elif kind == "lam":
                    v.wait_ge(small_in, 16 * 8)
                    for q in range(2):
                        v.tensor_tensor_reduce(lamrow[:, 256:320] if q == 0 else lamrow[:, 0:64],
                                               lamrow[:, 128 * q:128 * q + 64], lamrow[:, 128 * q + 64:128 * q + 128],
                                               1.0, 0.0, ALU.mult, ALU.add, lam2[0:1, q:q + 1]).then_inc(lam_sums, 1)
                        v.wait_ge(lam_sums, q + 1)
                    v.wait_ge(lam_exps, 1)
                    v.scalar_tensor_tensor(out=lam1[0:1, :], in0=lam2[0:1, 1:2], scalar=-LAMBDA_INIT, in1=lam2[0:1, 0:1],
                                           op0=ALU.add, op1=ALU.subtract).then_inc(lam_ready, 1)
                    ready(v, s)
                    own(v.tensor_copy(nlam, ps(s)[:, 0:1]))
                    v.sem_inc(bank_free[job_at[s][0]], 1)
                elif kind == "angles":
                    own(v.tensor_copy(pos_f, pos_i[:, :]))
                    own(v.tensor_tensor(ang.rearrange("p (b j) -> p b j", b=NB), pos_f.unsqueeze(2).broadcast_to([P, NB, RH]),
                                        ifreq.unsqueeze(1).broadcast_to([P, NB, RH]), ALU.mult))
                    own(v.tensor_scalar(turns, ang, 1.0 / TWO_PI, None, ALU.mult))
                    own(v.tensor_scalar(turns, turns, ROUND, None, ALU.add))
                    own(v.tensor_scalar(turns, turns, ROUND, None, ALU.subtract))
                    for part in (PI_A, PI_B, PI_C):
                        own(v.tensor_scalar(red, turns, -part, None, ALU.mult))
                        own(v.tensor_tensor(ang, ang, red, ALU.add))
                    own(v.tensor_scalar(red, ang, -1.0, None, ALU.mult))
                    own(v.tensor_tensor(red, red, ang, ALU.max))
                    v.tensor_scalar(cos_t, red, -1.0, math.pi / 2, ALU.mult, ALU.add).then_inc(angles_ready, 1)
                    v.tensor_scalar(sin_t, ang, 3.1415925, -3.1415925, ALU.min, ALU.max).then_inc(angles_ready, 1)
                elif kind == "rope":
                    q = s[1]
                    v.wait_ge(qk_raw, NB * (q + 1))
                    v.wait_ge(trig_ready, 2)
                    for b in range(NB):
                        src = tokA[:, b, 512 * q:512 * q + 512].rearrange("p (g d) -> p g d", d=64)
                        x1, x2 = src[:, :, 0:RH], src[:, :, RH:2 * RH]
                        cb = cos_t[:, RH * b:RH * b + RH].unsqueeze(1).broadcast_to([P, 8, RH])
                        sb_ = sin_t[:, RH * b:RH * b + RH].unsqueeze(1).broadcast_to([P, 8, RH])
                        tmp = [abuf[:, 0, 64 * j:64 * j + 64].rearrange("p (g d) -> p g d", d=RH) for j in range(4)]
                        for t_, (x_, y_) in zip(tmp, ((x1, cb), (x2, sb_), (x2, cb), (x1, sb_))):
                            ins = v.tensor_tensor(t_, x_, y_, ALU.mult)
                        own(ins)
                        v.tensor_tensor(x1, tmp[0], tmp[1], ALU.subtract)
                        own(v.tensor_tensor(x2, tmp[2], tmp[3], ALU.add))
                    v.sem_inc(roped, 1)
                elif kind == "qkT" and s[1] == 1:
                    ready(v, s)
                    dve_evac(v, v.tensor_copy(kT[:, s[2], :], ps(s)[:, :]), s, kT_ready)
                elif kind == "gate_z":
                    t = s[1]
                    ready(v, s)
                    own(v.tensor_scalar(decay[:, t, :], ps(s)[:, :], gcol[:, G_BA + t:G_BA + t + 1], None, ALU.add))
                    v.sem_inc(bank_free[job_at[s][0]], 1)
                elif kind == "gla_decay":
                    t = s[1]
                    z = decay[:, t, :]
                    v.scalar_tensor_tensor(out=qE[:, t, :], in0=z, scalar=-1.0, in1=z, op0=ALU.mult,
                                           op1=ALU.max).then_inc(abs_ready, 1)
                    v.wait_ge(softplus_ready, t + 1)
                    own(v.scalar_tensor_tensor(out=qE[:, t, :], in0=z, scalar=0.0, in1=kE[:, t, :], op0=ALU.min, op1=ALU.subtract))
                    own(v.tensor_scalar(qE[:, t, :], qE[:, t, :], 1.0 / GLA_TAU, None, ALU.mult))
                    for c in range(4):
                        ins = v.tensor_tensor_scan(decay[:, t, P * c:P * c + P], ones[:, :], qE[:, t, P * c:P * c + P],
                                                   0.0, ALU.mult, ALU.add)
                    own(ins)
                    d3 = decay[:, t, :].rearrange("p (c n) -> p c n", c=4)
                    mid, last = d3[:, :, 63:64].broadcast_to([P, 4, P]), d3[:, :, 127:128].broadcast_to([P, 4, P])
                    k3 = kE[:, t, :].rearrange("p (c n) -> p c n", c=4)
                    own(v.tensor_tensor(k3, d3, mid, ALU.subtract))
                    v.tensor_scalar(kE[:, t, :], kE[:, t, :], GUARD, -GUARD, ALU.min, ALU.max).then_inc(expo_ready, 1)
                    if t:
                        v.wait_ge(gla_ready, t)
                    v.tensor_tensor(ebuf[:, 0, :].rearrange("p (c n) -> p c n", c=4), last, d3, ALU.subtract).then_inc(expo_ready, 1)
                    v.wait_ge(decays_ready, t + 1)
                    v.wait_ge(gqk_ready, 4)
                    q_, k_ = gqkT[:, t, :], gqkT[:, 2 + t, :]
                    v.tensor_copy(dstate[:, 4 * t:4 * t + 4], ebuf[:, 1, :].rearrange("p (c n) -> p c n", c=4)[:, :, 127])
                    v.tensor_tensor(qE[:, t, :], qE[:, t, :], q_, ALU.mult)
                    own(v.tensor_tensor(kE[:, t, :], kE[:, t, :], k_, ALU.mult))
                    v.tensor_tensor(q_, q_, ebuf[:, 1, :], ALU.mult)
                    own(v.tensor_tensor(k_, k_, ebuf[:, 0, :], ALU.mult))
                    v.sem_inc(gla_ready, 1)
                elif kind == "proj" and s[1] == "gr":
                    b = s[2]
                    e_ = gr_tok[:, b, :]
                    v.wait_ge(gr_exp, b + 1)
                    own(v.tensor_scalar(e_, e_, 1.0, None, ALU.add))
                    own(v.reciprocal(e_, e_))
                    own(v.tensor_tensor(e_, e_, ps(s)[:, :], ALU.mult))
                    v.sem_inc(bank_free[job_at[s][0]], 1)
                elif kind == "norm_mem":
                    v.wait_ge(mrstd_ready, 1)
                    for b in range(MB):
                        v.tensor_scalar(mem_x[:, b, :], mem_x[:, b, :], mrstd[:, b:b + 1], None, ALU.mult).then_inc(memn_ready, 1)
                    for k in range(0, KT, 2):
                        j = s + (k,)
                        ready(v, j)
                        g2 = gcol[:, G_MEM + k:G_MEM + k + 2].unsqueeze(2).broadcast_to([P, 2, M])
                        dve_evac(v, v.tensor_tensor(memT[:, k:k + 2, :], ps(j)[:, :].rearrange("p (k n) -> p k n", k=2), g2, ALU.mult), j, memT_ready)
                elif kind == "proj" and s[1] == "kx":
                    ready(v, s)
                    dve_evac(v, v.tensor_copy(kxT[:, s[2], :], ps(s)[:, 0:M]), s, kx_ready)
                elif kind == "proj" and s[1] in ("wo", "co"):
                    g_, b = s[2] // 4, s[2] % 4
                    ready(v, s)
                    xr = x_res[:, b, 512 * g_:512 * g_ + 512]
                    dve_evac(v, v.tensor_tensor(xr, xr, ps(s)[:, :], ALU.add), s, res_ready)
                elif kind == "scores":
                    n, i = s[1], s[1] % 4
                    for c in range(2):
                        j = s + (c,)
                        ready(v, j)
                        dg = ps(j)[:, P * i:P * i + P]
                        own(v.tensor_tensor(dg, dg, negmask[:, :], ALU.add))
                        v.tensor_reduce(nmax[:, 2 * n + c:2 * n + c + 1], ps(j)[:, 0:P * (i + 1)], AX.X, ALU.max,
                                        negate=True).then_inc(max_ready, 1)
                elif kind == "combine":
                    n, i = s[1], s[1] % 4
                    w = P * (i + 1)
                    v.wait_ge(p_ready, 2 * n + 2)
                    own(v.reciprocal(rec[:, 2 * n:2 * n + 2], psum_[:, 2 * n:2 * n + 2]))
                    own(v.tensor_scalar(pbuf[:, 1, 0:w], pbuf[:, 1, 0:w], rec[:, 2 * n + 1:2 * n + 2], nlam, ALU.mult, ALU.mult))
                    if n >= 2:
                        ready(v, ("attnT", n - 2))
                    v.scalar_tensor_tensor(out=abuf[:, n % 2, 0:w], in0=pbuf[:, 0, 0:w], scalar=rec[:, 2 * n:2 * n + 1],
                                           in1=pbuf[:, 1, 0:w], op0=ALU.mult, op1=ALU.add).then_inc(a_ready, 1)
                elif kind == "gla_scores":
                    t = s[2]
                    ready(v, s)
                    own(v.tensor_scalar(gsc[:, t, :], ps(s)[:, 0:256], -NEG, NEG, ALU.min, ALU.max))
                    v.sem_inc(bank_free[job_at[s][0]], 1)
                    g3 = gsc[:, t, :].rearrange("p (u n) -> p u n", u=2)
                    v.tensor_tensor(g3, g3, keepT[:, :].unsqueeze(1).broadcast_to([P, 2, P]), ALU.mult).then_inc(gsc_ready, 1)
                elif kind == "gla_state":
                    c, t = s[1], s[2]
                    ready(v, s)
                    for hh in range(2):
                        r = slice(64 * hh, 64 * hh + 64)
                        new = ps(s)[r, P * hh:P * hh + P]
                        if c == 0:
                            ins = v.tensor_copy(state[r, t, :], new)
                        else:
                            ins = v.scalar_tensor_tensor(out=state[r, t, :], in0=state[r, t, :], scalar=dstate[r, 4 * t + c:4 * t + c + 1],
                                                         in1=new, op0=ALU.mult, op1=ALU.add)
                        ins.then_inc(state_ready, 1)
                    v.wait_ge(state_ready, 2 * (2 * c + t + 1))
                    v.sem_inc(bank_free[job_at[s][0]], 1)
                elif kind == "mix_norm":
                    v.wait_ge(orstd_ready, 1)
                    for b in range(NB):
                        half = tokA[:, b, 512:1024]
                        own(v.tensor_tensor(half, half, gr_tok[:, b, :], ALU.mult))
                        o3 = tokA[:, b, :].rearrange("p (h n) -> p h n", h=8)
                        r3 = orstd.rearrange("p (h b) -> p h b", b=4)[:, :, b:b + 1].broadcast_to([P, 8, P])
                        v.tensor_tensor(o3, o3, r3, ALU.mult).then_inc(mixed_ready, 1)
                elif kind == "oT":
                    for k in range(1, KT, 2):
                        j = s + (k,)
                        ready(v, j)
                        gc = G_DA if k < 4 else G_GLA
                        dve_evac(v, v.tensor_scalar(actT[:, k, :], ps(j)[:, :], gcol[:, gc:gc + 1], None, ALU.mult), j, actT_ready)
                elif kind == "xscores":
                    h, i = s[1], s[2]
                    n = 4 * h + i
                    ready(v, s)
                    v.tensor_reduce(nmax[:, n:n + 1], ps(s)[:, 0:M], AX.X, ALU.max, negate=True).then_inc(xmax_ready, 1)
                    if n:
                        xnormal(v, s, n - 1)
                    if n == 15:
                        xnormal(v, s, n)
                elif kind == "xT" and s[2] == 1:
                    ready(v, s)
                    dve_evac(v, v.tensor_copy(xpT[:, s[1] % 2, 1, :], ps(s)[:, :]), s, xpT_ready)
                elif kind == "xout" and s[2] == 1:
                    ready(v, s)
                    dve_evac(v, v.tensor_copy(actT[:, 2 * s[1] + 1, :], ps(s)[:, :]), s, actT_ready)
                elif kind == "router":
                    j = s + ("logits",)
                    ready(v, j)
                    own(v.tensor_copy(lg[:, :, :], ps(j)[:, 0:P].rearrange("p (b e) -> p b e", b=NB)))
                    v.sem_inc(bank_free[job_at[j][0]], 1)
                elif kind == "route":
                    m8 = mx8.rearrange("p (b k) -> p b k", b=NB)
                    i4 = idxf.rearrange("p (b k) -> p b k", b=NB)
                    g4 = gate4.rearrange("p (b k) -> p b k", b=NB)
                    for b in range(NB):
                        own(v.max(m8[:, b, :], lg[:, b, :]))
                        own(v.max_index(idx8[:, b, :], m8[:, b, :], lg[:, b, :]))
                    v.tensor_tensor(g4, m8[:, :, 0:TOP], m8[:, :, 0:1].broadcast_to([P, NB, TOP]), ALU.subtract).then_inc(gexp_in, 1)
                    own(v.tensor_copy(i4, idx8[:, :, 0:TOP]))
                    hit = pbuf.rearrange("p u n -> p (u n)")[:, 0:NB * NE * TOP].rearrange("p (b e k) -> p b e k", b=NB, e=NE)
                    for b in range(NB):
                        ins = v.tensor_tensor(hit[:, b, :, :], iota_e[:, :].unsqueeze(2).broadcast_to([P, NE, TOP]),
                                              i4[:, b:b + 1, :].broadcast_to([P, NE, TOP]), ALU.is_equal)
                    own(ins)
                    own(v.tensor_reduce(m_f[:, :, :], hit, AX.X, ALU.add))
                    v.tensor_copy(slot_m[:, :, :], m_f[:, :, :]).then_inc(m_ready, 1)
                    v.wait_ge(gexp_ready, 1)
                    own(v.tensor_reduce(gsum, g4, AX.X, ALU.add))
                    own(v.reciprocal(gsum, gsum))
                    own(v.tensor_tensor(g4, g4, gsum.unsqueeze(2).broadcast_to([P, NB, TOP]), ALU.mult))
                    for b in range(NB):
                        ins = v.tensor_tensor(hit[:, b, :, :], hit[:, b, :, :], g4[:, b:b + 1, :].broadcast_to([P, NE, TOP]), ALU.mult)
                    own(ins)
                    own(v.tensor_reduce(g_f[:, :, :], hit, AX.X, ALU.add))
                    for b in range(NB):
                        v.tensor_copy(slot_src[:, b, 0:NE, 0], part_f.broadcast_to([P, NE]))
                        v.tensor_scalar(slot_src[:, b, 0:NE, 1], iota_e[:, :], 0.0, P * b - OOB, ALU.mult, ALU.add)
                    for q in range(3):
                        own(v.tensor_copy(slot_src[:, :, 0:NE, 2 + q], g_f[:, :, :]))
                        if q < 2:
                            own(v.tensor_tensor(g_f[:, :, :], g_f[:, :, :], slot_src[:, :, 0:NE, 2 + q], ALU.subtract))
                    j = s + ("rank",)
                    ready(v, j)
                    r_ = slot_rank[:, :, 0:NE]
                    own(v.scalar_tensor_tensor(out=r_, in0=ps(j)[:, 0:P].rearrange("p (b e) -> p b e", b=NB), scalar=1.0,
                                               in1=m_f[:, :, :], op0=ALU.add, op1=ALU.mult))
                    v.sem_inc(bank_free[job_at[j][0]], 1)
                    own(v.tensor_scalar(r_, r_, -1.0, None, ALU.add))
                    j = s + ("count",)
                    ready(v, j)
                    own(v.tensor_copy(count_f[:, :], ps(j)[0:1, 0:NE]))
                    v.sem_inc(bank_free[job_at[j][0]], 1)
                    v.sem_inc(slots_ready, 1)

            main, prep = Steps(dve_main), Steps(dve_prep)

            def own_in(steps_, ins):
                steps_.mark(ins)
                steps_.wait(v)

            def slots_of(pn, e, j):
                for b in range(NB):
                    ins = v.tensor_scalar(onehot[:, b, :], iota_s[:, bass.ds(j * W, W)] if j is not None else iota_s[:, 0:W],
                                          slot_rank[:, b, bass.ds(e, 1)], None, ALU.is_equal)
                ins.then_inc(onehot_ready, 1)

            def rows_of(pn):
                v.wait_ge(idx_done, pn + 1)
                v.tensor_reduce(gate_next[0:W, :], bank[7][0:W, 2:5], AX.X, ALU.add)
                own_in(prep, v.tensor_reduce(idx_f[0:W, :], bank[7][0:W, 0:2], AX.X, ALU.add))
                v.tensor_scalar(idx_next[0:W, :], idx_f[0:W, :], OOB, None, ALU.add).then_inc(idx_ready, 1)

            def rows_T_out(pn):
                v.wait_ge(xgT_done, pn + 1)
                v.tensor_copy(xT[:, 4:8, :], bank[7][:, 0:4 * W].rearrange("p (k n) -> p k n", k=4)).then_inc(xT_ready, 1)

            def select(n, e):
                v.wait_ge(down_full, 2 * n + 2)
                v.tensor_scalar(sel, ones[:, 0:W], part_of[:, bass.ds(e, 1)], None, ALU.mult).then_inc(sel_ready, 1)

            def swiglu(n, p):
                u = p % 2
                v.wait_ge(up_full, n * PANELS + (p + 1))
                if p >= 2:
                    v.wait_ge(hT_done, n * PANELS + (p - 1))
                v.tensor_scalar(glu[0:W, u, :], bank[p][0:W, 0:256], LIMIT, None, ALU.min).then_inc(glu_ready, 1)
                own_in(main, v.tensor_scalar(lin[0:W, u, :], bank[p][0:W, 256:512], LIMIT, -LIMIT, ALU.min, ALU.max))
                v.sem_inc(up_free, 1)
                v.wait_ge(glu_ready, n * PANELS + (p + 1))
                own_in(main, v.scalar_tensor_tensor(out=lin[0:W, u, :], in0=lin[0:W, u, :], scalar=1.0, in1=glu[0:W, u, :],
                                                    op0=ALU.add, op1=ALU.mult))
                v.wait_ge(sig_ready, n * PANELS + (p + 1))
                v.tensor_tensor(act_tok[0:W, u, :], lin[0:W, u, :], sig[0:W, u, :], ALU.mult).then_inc(act_ready, 1)

            def to_current(n):
                v.wait_ge(cur_free, n + 1)
                v.tensor_copy(idx_cur[0:W, :], idx_next[0:W, :])
                own_in(main, v.tensor_copy(gate_cur[0:W, :], gate_next[0:W, :]))
                v.sem_inc(cur_ready, 1)

            v.sem_inc(up_free, PANELS)
            v.wait_ge(iota_ready, 1)
            slots_of(0, 0, None)
            rows_of(0)
            own(v.memset(ovf_n, 0.0))
            for j in range(1, T // W):
                own(v.scalar_tensor_tensor(out=ovf_n, in0=count_f[:, :], scalar=float(j * W), in1=ovf_n,
                                           op0=ALU.is_gt, op1=ALU.add))
            own(v.tensor_tensor_scan(ovf_upto, ones[0:1, 0:NE], ovf_n, 0.0, ALU.mult, ALU.add))
            le = pbuf_row.rearrange("p (m e) -> p m e", e=NE)
            st = abuf_row.rearrange("p (m e) -> p m e", e=NE)
            upto = ovf_upto.unsqueeze(1).broadcast_to([1, MO, NE])
            own(v.tensor_tensor(le, upto, iota_s[0:1, 0:MO].unsqueeze(2).broadcast_to([1, MO, NE]), ALU.is_le))
            own(v.tensor_tensor(st, le, upto, ALU.mult))
            own(v.tensor_reduce(ovf_e, le, AX.X, ALU.add))
            own(v.tensor_reduce(ovf_j, st, AX.X, ALU.max))
            own(v.scalar_tensor_tensor(out=ovf_j, in0=iota_s[0:1, 0:MO], scalar=1.0, in1=ovf_j, op0=ALU.add, op1=ALU.subtract))
            v.tensor_copy(ovf[:, 0:MO], ovf_e)
            v.tensor_copy(ovf[:, MO:2 * MO], ovf_j)
            own(v.tensor_copy(ovf[:, 2 * MO:2 * MO + 1], ovf_upto[:, NE - 1:NE]))
            v.sem_inc(table_ready, 1)
            rows_T_out(0)
            prep_each, main_each = 1, 2 * PANELS + 1
            with v.Fori(0, NE) as e:
                main.base, main.n = e * main_each, 0
                prep.base, prep.n = e + 1, 0
                select(e, e)
                slots_of(e + 1, e + 1, None)
                swiglu(e, 0)
                swiglu(e, 1)
                to_current(e)
                rows_of(e + 1)
                swiglu(e, 2)
                swiglu(e, 3)
                rows_T_out(e + 1)
                assert (main.n, prep.n) == (main_each, prep_each)
            extra = v.value_load(ovf[0:1, 2 * MO:2 * MO + 1], min_val=0, max_val=MO)
            with v.If(extra > 0):
                with v.Fori(0, extra) as m:
                    e = v.value_load(ovf[0:1, bass.ds(m, 1)], min_val=0, max_val=NE - 1)
                    j = v.value_load(ovf[0:1, bass.ds(m + MO, 1)], min_val=1, max_val=T // W - 1)
                    main.base, main.n = m * main_each + NE * main_each, 0
                    prep.base, prep.n = m + (NE + 1), 0
                    slots_of(m + (NE + 1), e, j)
                    rows_of(m + (NE + 1))
                    rows_T_out(m + (NE + 1))
                    select(m + NE, e)
                    swiglu(m + NE, 0)
                    swiglu(m + NE, 1)
                    to_current(m + NE)
                    swiglu(m + NE, 2)
                    swiglu(m + NE, 3)
            v.wait_ge(gfin_in, 16)
            for b in range(NB):
                v.wait_ge(fin_rstd, b + 1)
                v.scalar_tensor_tensor(out=x_res[:, b, :], in0=x_res[:, b, :], scalar=rstd[:, b:b + 1], in1=gfin,
                                       op0=ALU.mult, op1=ALU.mult).then_inc(fin_ready, 1)


_INS = ["x", "mem", "positions", "norm_mix_g", "w_in", "lambda_q1", "lambda_k1", "lambda_q2", "lambda_k2",
        "diff_norm_g", "w_alpha2", "b_alpha", "gla_norm_g", "w_out", "norm_cross_g", "norm_mem_g", "w_cq", "w_ck",
        "w_cv", "w_co", "norm_ffn_g", "w_router", "b_router", "w_up", "b_up", "w_down", "b_down", "norm_final_g"]


def kernel(**inputs):
    import numpy as _np
    import concourse.bacc as _bacc
    from concourse import mybir as _mybir
    from concourse.bass_utils import run_bass_kernel_spmd as _run

    nc = _bacc.Bacc("TRN2", target_bir_lowering=False, num_devices=1)
    arrays, aps = {}, {}
    for name in _INS:
        a = _np.ascontiguousarray(inputs[name])
        arrays[f"in_{name}"] = a
        aps[name] = nc.dram_tensor(f"in_{name}", a.shape, _mybir.dt.from_np(a.dtype), kind="ExternalInput").ap()
    aps["out"] = nc.dram_tensor("out_0", inputs["x"].shape, _mybir.dt.float32, kind="ExternalOutput").ap()
    decoder_block(nc, aps)
    r = _run(nc, [arrays], core_ids=[0])
    return r.results[0]["out_0"]
```
